# Optimizing a Trainium2 kernel written in Bass

```python
import jax, jax.numpy as jnp
from jax import lax
import numpy as np

D_MODEL = 2048
BATCH = 1
SEQ = 256
DEPTH = 1

N_MIXERS = 4
HEAD_DIM = 128
N_HEADS = D_MODEL // HEAD_DIM
Q_BLOCK = 128
EPS = 1e-6

FOX_FGATE_BIAS = 2.0

MLA_Q_RANK = 512
MLA_KV_RANK = 512
MLA_NOPE = 128
MLA_ROPE = 64
MLA_V = 128
ROPE_THETA = 10000.0

SGU_CHUNK = 128
SGU_WIDTH = D_MODEL
SGU_GROUP_DIM = 128
SGU_GROUPS = SGU_WIDTH // SGU_GROUP_DIM

D_FF = 5632
CONV_WIDTH = 3


def _n_layers_of(m):
    return len(range(m, DEPTH, N_MIXERS))

def rms_norm(x, gain):
    x32 = x.astype(jnp.float32)
    y = x32 * lax.rsqrt(jnp.mean(x32 * x32, axis=-1, keepdims=True) + EPS)
    return (y * gain.astype(jnp.float32)).astype(x.dtype)

def _sweep_query_blocks(block_fn, seq):
    out = lax.map(block_fn, jnp.arange(seq // Q_BLOCK))
    nb, b, qb, h, dv = out.shape
    return out.transpose(1, 0, 2, 3, 4).reshape(b, seq, h * dv)

def _causal_softmax(s, start, v):
    seq = s.shape[-1]
    q_pos = start + jnp.arange(Q_BLOCK)
    allowed = jnp.arange(seq)[None, :] <= q_pos[:, None]
    p = jax.nn.softmax(jnp.where(allowed, s, -jnp.inf), axis=-1)
    return jnp.einsum('bhqs,bshd->bqhd', p.astype(v.dtype), v)

def fox_mixer(h, w_in, b_f, q_gain, k_gain, w_out):
    bsz, seq, _ = h.shape
    hd = N_HEADS * HEAD_DIM
    q, k, v, f_logit = jnp.split(h @ w_in, [hd, 2 * hd, 3 * hd], axis=-1)
    q = rms_norm(q.reshape(bsz, seq, N_HEADS, HEAD_DIM), q_gain)
    k = rms_norm(k.reshape(bsz, seq, N_HEADS, HEAD_DIM), k_gain)
    v = v.reshape(bsz, seq, N_HEADS, HEAD_DIM)
    log_f = jax.nn.log_sigmoid(f_logit.astype(jnp.float32) + b_f.astype(jnp.float32))
    cum = jnp.cumsum(log_f, axis=1).transpose(0, 2, 1)
    scale = HEAD_DIM ** -0.5

    def block(i):
        start = i * Q_BLOCK
        qb = lax.dynamic_slice_in_dim(q, start, Q_BLOCK, axis=1)
        cq = lax.dynamic_slice_in_dim(cum, start, Q_BLOCK, axis=2)
        s = jnp.einsum('bqhd,bshd->bhqs', qb, k, preferred_element_type=jnp.float32) * scale
        s = s + (cq[..., :, None] - cum[:, :, None, :])
        return _causal_softmax(s, start, v)

    return _sweep_query_blocks(block, seq) @ w_out

def _rope_tables(positions):
    inv_freq = ROPE_THETA ** (-jnp.arange(0, MLA_ROPE, 2, dtype=jnp.float32) / MLA_ROPE)
    ang = positions.astype(jnp.float32)[..., None] * inv_freq
    return jnp.cos(ang)[:, :, None, :], jnp.sin(ang)[:, :, None, :]

def _apply_rope(x, cos, sin):
    x1, x2 = jnp.split(x.astype(jnp.float32), 2, axis=-1)
    return jnp.concatenate([x1 * cos - x2 * sin, x1 * sin + x2 * cos], axis=-1).astype(x.dtype)

def mla_mixer(h, positions, w_in, q_a_gain, kv_a_gain, w_q_b, w_kv_b, q_gain, k_gain, w_out):
    bsz, seq, _ = h.shape
    c_q, c_kv, k_rope = jnp.split(h @ w_in, [MLA_Q_RANK, MLA_Q_RANK + MLA_KV_RANK], axis=-1)
    q = (rms_norm(c_q, q_a_gain) @ w_q_b).reshape(bsz, seq, N_HEADS, MLA_NOPE + MLA_ROPE)
    kv = (rms_norm(c_kv, kv_a_gain) @ w_kv_b).reshape(bsz, seq, N_HEADS, MLA_NOPE + MLA_V)
    q_nope, q_rope = jnp.split(q, [MLA_NOPE], axis=-1)
    k_nope, v = jnp.split(kv, [MLA_NOPE], axis=-1)
    cos, sin = _rope_tables(positions)
    q_nope = rms_norm(q_nope, q_gain[:MLA_NOPE])
    k_nope = rms_norm(k_nope, k_gain[:MLA_NOPE])
    q_rope = _apply_rope(rms_norm(q_rope, q_gain[MLA_NOPE:]), cos, sin)
    k_rope = _apply_rope(rms_norm(k_rope[:, :, None, :], k_gain[MLA_NOPE:]), cos, sin)
    q = jnp.concatenate([q_nope, q_rope], axis=-1)
    k = jnp.concatenate([k_nope, jnp.broadcast_to(k_rope, (bsz, seq, N_HEADS, MLA_ROPE))], axis=-1)
    scale = (MLA_NOPE + MLA_ROPE) ** -0.5

    def block(i):
        start = i * Q_BLOCK
        qb = lax.dynamic_slice_in_dim(q, start, Q_BLOCK, axis=1)
        s = jnp.einsum('bqhd,bshd->bhqs', qb, k, preferred_element_type=jnp.float32) * scale
        return _causal_softmax(s, start, v)

    return _sweep_query_blocks(block, seq) @ w_out

def stick_breaking_mixer(h, w_in, q_gain, k_gain, w_out):
    bsz, seq, _ = h.shape
    hd = N_HEADS * HEAD_DIM
    q, k, v = jnp.split(h @ w_in, [hd, 2 * hd], axis=-1)
    q = rms_norm(q.reshape(bsz, seq, N_HEADS, HEAD_DIM), q_gain)
    k = rms_norm(k.reshape(bsz, seq, N_HEADS, HEAD_DIM), k_gain)
    v = v.reshape(bsz, seq, N_HEADS, HEAD_DIM)
    scale = HEAD_DIM ** -0.5

    def block(i):
        start = i * Q_BLOCK
        qb = lax.dynamic_slice_in_dim(q, start, Q_BLOCK, axis=1)
        z = jnp.einsum('bqhd,bshd->bhqs', qb, k, preferred_element_type=jnp.float32) * scale
        q_pos = start + jnp.arange(Q_BLOCK)
        strict = jnp.arange(seq)[None, :] < q_pos[:, None]
        log_keep = jnp.where(strict, -jax.nn.softplus(z), 0.0)
        after = lax.cumsum(log_keep, axis=3, reverse=True) - log_keep
        a = jnp.where(strict, jnp.exp(jax.nn.log_sigmoid(z) + after), 0.0)
        return jnp.einsum('bhqs,bshd->bqhd', a.astype(v.dtype), v)

    return _sweep_query_blocks(block, seq) @ w_out

def sgu_mixer(h, w_in, v_gain, w_s, b_s, w_out):
    bsz, seq, _ = h.shape
    u, vv = jnp.split(jax.nn.gelu(h @ w_in), 2, axis=-1)
    vv = rms_norm(vv, v_gain)
    n_chunks = seq // SGU_CHUNK
    vv = vv.reshape(bsz, n_chunks, SGU_CHUNK, SGU_GROUPS, SGU_GROUP_DIM)
    causal = jnp.tril(jnp.ones((SGU_CHUNK, SGU_CHUNK), dtype=bool))
    ws = jnp.where(causal[None], w_s, 0.0).astype(vv.dtype)
    mixed = jnp.einsum('gts,bnsgc->bntgc', ws, vv) + b_s.T[:, :, None]
    return (u * mixed.reshape(bsz, seq, SGU_WIDTH)) @ w_out

def conv_ffn(h, w_up, conv_w, conv_b, w_down):
    seq = h.shape[1]
    up = h @ w_up
    padded = jnp.pad(up, ((0, 0), (CONV_WIDTH - 1, 0), (0, 0)))
    y = conv_b + conv_w[0] * padded[:, 0:seq]
    for tap in range(1, CONV_WIDTH):
        y = y + conv_w[tap] * padded[:, tap:tap + seq]
    gate, val = jnp.split(y, 2, axis=-1)
    return (jax.nn.silu(gate) * val) @ w_down

def first_inputs(seed: int = 0) -> dict:
    key = jax.random.key(seed)
    ks = iter(list(jax.random.split(key, 32)))

    def w(shape, fan_in):
        return jax.random.normal(next(ks), shape, jnp.float32) * fan_in ** -0.5

    def gain(shape):
        return 1.0 + 0.1 * jax.random.normal(next(ks), shape, jnp.float32)

    n_a, n_b, n_c, n_d = (_n_layers_of(m) for m in range(N_MIXERS))
    hd = N_HEADS * HEAD_DIM
    x = jax.random.normal(next(ks), (BATCH, SEQ, D_MODEL), jnp.float32)
    offset = jax.random.randint(next(ks), (BATCH, 1), 0, 4096, dtype=jnp.int32)
    positions = offset + jnp.arange(SEQ, dtype=jnp.int32)[None, :]
    return {
        'x': x,
        'positions': positions,
        'mix_norm': gain((DEPTH, D_MODEL)),
        'ffn_norm': gain((DEPTH, D_MODEL)),
        'fox_w_in': w((n_a, D_MODEL, 3 * hd + N_HEADS), D_MODEL),
        'fox_b_f': FOX_FGATE_BIAS + 0.5 * jax.random.normal(next(ks), (n_a, N_HEADS), jnp.float32),
        'fox_q_gain': gain((n_a, HEAD_DIM)),
        'fox_k_gain': gain((n_a, HEAD_DIM)),
        'fox_w_out': w((n_a, hd, D_MODEL), hd),
        'mla_w_in': w((n_b, D_MODEL, MLA_Q_RANK + MLA_KV_RANK + MLA_ROPE), D_MODEL),
        'mla_q_a_gain': gain((n_b, MLA_Q_RANK)),
        'mla_kv_a_gain': gain((n_b, MLA_KV_RANK)),
        'mla_w_q_b': w((n_b, MLA_Q_RANK, N_HEADS * (MLA_NOPE + MLA_ROPE)), MLA_Q_RANK),
        'mla_w_kv_b': w((n_b, MLA_KV_RANK, N_HEADS * (MLA_NOPE + MLA_V)), MLA_KV_RANK),
        'mla_q_gain': gain((n_b, MLA_NOPE + MLA_ROPE)),
        'mla_k_gain': gain((n_b, MLA_NOPE + MLA_ROPE)),
        'mla_w_out': w((n_b, N_HEADS * MLA_V, D_MODEL), N_HEADS * MLA_V),
        'sb_w_in': w((n_c, D_MODEL, 3 * hd), D_MODEL),
        'sb_q_gain': gain((n_c, HEAD_DIM)),
        'sb_k_gain': gain((n_c, HEAD_DIM)),
        'sb_w_out': w((n_c, hd, D_MODEL), hd),
        'sgu_w_in': w((n_d, D_MODEL, 2 * SGU_WIDTH), D_MODEL),
        'sgu_v_gain': gain((n_d, SGU_WIDTH)),
        'sgu_w_s': w((n_d, SGU_GROUPS, SGU_CHUNK, SGU_CHUNK), SGU_CHUNK),
        'sgu_b_s': gain((n_d, SGU_GROUPS, SGU_CHUNK)),
        'sgu_w_out': w((n_d, SGU_WIDTH, D_MODEL), SGU_WIDTH),
        'ffn_w_up': w((DEPTH, D_MODEL, 2 * D_FF), D_MODEL),
        'ffn_conv_w': w((DEPTH, CONV_WIDTH, 2 * D_FF), CONV_WIDTH),
        'ffn_conv_b': 0.01 * jax.random.normal(next(ks), (DEPTH, 2 * D_FF), jnp.float32),
        'ffn_w_down': w((DEPTH, D_FF, D_MODEL), D_FF),
    }

def first_block(x, positions, mix_norm, ffn_norm,
              fox_w_in, fox_b_f, fox_q_gain, fox_k_gain, fox_w_out,
              mla_w_in, mla_q_a_gain, mla_kv_a_gain, mla_w_q_b, mla_w_kv_b,
              mla_q_gain, mla_k_gain, mla_w_out,
              sb_w_in, sb_q_gain, sb_k_gain, sb_w_out,
              sgu_w_in, sgu_v_gain, sgu_w_s, sgu_b_s, sgu_w_out,
              ffn_w_up, ffn_conv_w, ffn_conv_b, ffn_w_down):
    h = x
    for i in range(DEPTH):
        m, j = i % N_MIXERS, i // N_MIXERS
        a = rms_norm(h, mix_norm[i])
        if m == 0:
            mixed = fox_mixer(a, fox_w_in[j], fox_b_f[j], fox_q_gain[j], fox_k_gain[j], fox_w_out[j])
        elif m == 1:
            mixed = mla_mixer(a, positions, mla_w_in[j], mla_q_a_gain[j], mla_kv_a_gain[j],
                              mla_w_q_b[j], mla_w_kv_b[j], mla_q_gain[j], mla_k_gain[j], mla_w_out[j])
        elif m == 2:
            mixed = stick_breaking_mixer(a, sb_w_in[j], sb_q_gain[j], sb_k_gain[j], sb_w_out[j])
        else:
            mixed = sgu_mixer(a, sgu_w_in[j], sgu_v_gain[j], sgu_w_s[j], sgu_b_s[j], sgu_w_out[j])
        h = h + mixed
        h = h + conv_ffn(rms_norm(h, ffn_norm[i]), ffn_w_up[i], ffn_conv_w[i], ffn_conv_b[i], ffn_w_down[i])
    return h


MIX_WIDTH = D_MODEL
GLA_HEADS = 4
GLA_DV = MIX_WIDTH // 2 // GLA_HEADS
GLA_DK = GLA_DV // 2
GLA_GATE_RANK = 16
GLA_GATE_TAU = 16.0
GLA_CHUNK = 64
DIL_HEADS = 8
DIL_DH = (MIX_WIDTH - GLA_HEADS * GLA_DV) // DIL_HEADS
DIL_PATTERNS = ((128, 1), (512, 4), (2048, 16))
DIL_BLOCK = 128
REL_BUCKETS = 32
REL_MAX_DIST = 2048
FFN_HIDDEN = -(-8 * D_MODEL // (3 * 256)) * 256
RMS_EPS = 1e-6
NEG_INF = -1e30

SPLIT_SIZES = (
    GLA_HEADS * GLA_DK,
    GLA_HEADS * GLA_DK,
    GLA_HEADS * GLA_DV,
    GLA_HEADS * GLA_DV,
    GLA_GATE_RANK,
    DIL_HEADS * DIL_DH,
    DIL_HEADS * DIL_DH,
    DIL_HEADS * DIL_DH,
)
N_IN = sum(SPLIT_SIZES)


def rms_norm_2(x, g):
    xf = x.astype(jnp.float32)
    y = xf * lax.rsqrt(jnp.mean(xf * xf, axis=-1, keepdims=True) + RMS_EPS)
    return (y * g.astype(jnp.float32)).astype(x.dtype)

def t5_bucket(dist):
    max_exact = REL_BUCKETS // 2
    safe = np.maximum(dist, 1)
    large = max_exact + (np.log(safe / max_exact) / np.log(REL_MAX_DIST / max_exact)
                         * (REL_BUCKETS - max_exact)).astype(np.int64)
    large = np.minimum(large, REL_BUCKETS - 1)
    return np.where(dist < max_exact, dist, large).astype(np.int32)

def gla_mixer(q, k, v, r, log_g, onorm_g):
    Bsz, S, H, DK = q.shape
    DV = v.shape[-1]
    C = GLA_CHUNK
    N = S // C

    def chunks(t):
        return t.astype(jnp.float32).reshape(Bsz, N, C, H, t.shape[-1]).transpose(0, 3, 1, 2, 4)

    qc = chunks(q) * (DK ** -0.5)
    kc, vc, gc = chunks(k), chunks(v), chunks(log_g)
    b = jnp.cumsum(gc, axis=3)
    q_t = qc * jnp.exp(b)
    k_t = kc * jnp.exp(-b)
    causal = np.tril(np.ones((C, C), dtype=bool))
    attn = jnp.einsum('bhnid,bhnjd->bhnij', q_t, k_t)
    attn = jnp.where(causal, attn, 0.0)
    o_intra = jnp.einsum('bhnij,bhnjv->bhniv', attn, vc)

    b_last = b[:, :, :, -1, :]
    k_dec = kc * jnp.exp(b_last[:, :, :, None, :] - b)
    chunk_state = jnp.einsum('bhncd,bhncv->bhndv', k_dec, vc)

    def step(state, inp):
        q_n, decay_n, cs_n = inp
        o_n = jnp.einsum('bhcd,bhdv->bhcv', q_n, state)
        state = decay_n[..., None] * state + cs_n
        return state, o_n

    init = jnp.zeros((Bsz, H, DK, DV), jnp.float32)
    xs = (q_t.transpose(2, 0, 1, 3, 4), jnp.exp(b_last).transpose(2, 0, 1, 3),
          chunk_state.transpose(2, 0, 1, 3, 4))
    _, o_inter = lax.scan(step, init, xs)
    o = o_intra + o_inter.transpose(1, 2, 0, 3, 4)
    o = o.transpose(0, 2, 3, 1, 4).reshape(Bsz, S, H, DV)
    o = rms_norm_2(o, onorm_g)
    o = o.reshape(Bsz, S, H * DV) * jax.nn.silu(r.astype(jnp.float32))
    return o

def dilated_branch(q, k, v, rel_bias, window, dilation):
    Bsz, H, S, Dh = q.shape
    span = window // dilation
    Q = DIL_BLOCK
    seg = dilation * Q
    Sp = -(-S // seg) * seg
    L = Sp // dilation
    nb = L // Q

    def to_blocks(t):
        t = jnp.pad(t, ((0, 0), (0, 0), (0, Sp - S), (0, 0)))
        return t.reshape(Bsz, H, L, dilation, Dh).transpose(0, 1, 3, 2, 4).reshape(Bsz, H, dilation, nb, Q, Dh)

    qb, kb, vb = to_blocks(q), to_blocks(k), to_blocks(v)
    blk_pad = ((0, 0), (0, 0), (0, 0), (1, 0), (0, 0), (0, 0))
    kk = jnp.concatenate([jnp.pad(kb[:, :, :, :-1], blk_pad), kb], axis=4)
    vv = jnp.concatenate([jnp.pad(vb[:, :, :, :-1], blk_pad), vb], axis=4)

    i = np.arange(Q)[:, None]
    j = np.arange(2 * Q)[None, :]
    rel = Q + i - j
    band = (rel >= 0) & (rel <= span)
    valid = band[None] & ((np.arange(nb)[:, None, None] > 0) | (j >= Q)[None])
    buckets = t5_bucket(np.clip(rel, 0, None) * dilation)
    bias = jnp.take(rel_bias.astype(jnp.float32), buckets, axis=0).transpose(2, 0, 1)

    logits = jnp.einsum('bhrnqd,bhrnkd->bhrnqk', qb, kk) * (Dh ** -0.5)
    logits = logits + bias[None, :, None, None]
    logits = jnp.where(valid[None, None, None], logits, NEG_INF)
    m = jnp.max(logits, axis=-1, keepdims=True)
    p = jnp.exp(logits - m)
    s = jnp.sum(p, axis=-1, keepdims=True)
    o = jnp.einsum('bhrnqk,bhrnkd->bhrnqd', p, vv) / s
    lse = (m + jnp.log(s))[..., 0]

    o = o.reshape(Bsz, H, dilation, L, Dh).transpose(0, 1, 3, 2, 4).reshape(Bsz, H, Sp, Dh)[:, :, :S]
    lse = lse.reshape(Bsz, H, dilation, L).transpose(0, 1, 3, 2).reshape(Bsz, H, Sp)[:, :, :S]
    return o, lse

def dilated_mixer(q, k, v, rel_bias):
    Bsz, S, H, Dh = q.shape
    qf, kf, vf = (t.astype(jnp.float32).transpose(0, 2, 1, 3) for t in (q, k, v))
    outs, lses = [], []
    for window, dilation in DIL_PATTERNS:
        o, lse = dilated_branch(qf, kf, vf, rel_bias, window, dilation)
        outs.append(o)
        lses.append(lse)
    w = jax.nn.softmax(jnp.stack(lses, axis=0), axis=0)
    o = jnp.sum(w[..., None] * jnp.stack(outs, axis=0), axis=0)
    return o.transpose(0, 2, 1, 3).reshape(Bsz, S, H * Dh)

def second_inputs(seed: int = 0) -> dict:
    key = jax.random.key(seed)
    ks = jax.random.split(key, 16)
    f32 = jnp.float32
    nrm = lambda k, shape, scale: jax.random.normal(k, shape, f32) * scale
    return {
        "x": nrm(ks[0], (BATCH, SEQ, D_MODEL), 1.0),
        "norm1_g": 1.0 + nrm(ks[1], (DEPTH, D_MODEL), 0.02),
        "w_in": nrm(ks[2], (DEPTH, D_MODEL, N_IN), D_MODEL ** -0.5),
        "gla_gate_w2": nrm(ks[3], (DEPTH, GLA_GATE_RANK, GLA_HEADS * GLA_DK), GLA_GATE_RANK ** -0.5),
        "gla_gate_b": nrm(ks[4], (DEPTH, GLA_HEADS * GLA_DK), 0.1),
        "gla_onorm_g": 1.0 + nrm(ks[5], (DEPTH, GLA_DV), 0.02),
        "q_norm_g": 1.0 + nrm(ks[6], (DEPTH, DIL_DH), 0.02),
        "k_norm_g": 1.0 + nrm(ks[7], (DEPTH, DIL_DH), 0.02),
        "rel_bias": nrm(ks[8], (REL_BUCKETS, DIL_HEADS), 0.5),
        "w_out": nrm(ks[9], (DEPTH, MIX_WIDTH, D_MODEL), MIX_WIDTH ** -0.5),
        "norm2_g": 1.0 + nrm(ks[10], (DEPTH, D_MODEL), 0.02),
        "w_gate": nrm(ks[11], (DEPTH, D_MODEL, FFN_HIDDEN), D_MODEL ** -0.5),
        "w_up": nrm(ks[12], (DEPTH, D_MODEL, FFN_HIDDEN), D_MODEL ** -0.5),
        "w_down": nrm(ks[13], (DEPTH, FFN_HIDDEN, D_MODEL), FFN_HIDDEN ** -0.5),
    }

def second_block(x, norm1_g, w_in, gla_gate_w2, gla_gate_b, gla_onorm_g, q_norm_g, k_norm_g,
              rel_bias, w_out, norm2_g, w_gate, w_up, w_down):
    Bsz, S, _ = x.shape
    split_points = list(np.cumsum(SPLIT_SIZES)[:-1])
    for l in range(DEPTH):
        h = rms_norm_2(x, norm1_g[l])
        proj = h @ w_in[l]
        qa, ka, va, ra, ga, qb, kb, vb = jnp.split(proj, split_points, axis=-1)
        gate_pre = (ga @ gla_gate_w2[l] + gla_gate_b[l]).astype(jnp.float32)
        log_g = jax.nn.log_sigmoid(gate_pre) / GLA_GATE_TAU
        out_a = gla_mixer(qa.reshape(Bsz, S, GLA_HEADS, GLA_DK),
                          ka.reshape(Bsz, S, GLA_HEADS, GLA_DK),
                          va.reshape(Bsz, S, GLA_HEADS, GLA_DV),
                          ra,
                          log_g.reshape(Bsz, S, GLA_HEADS, GLA_DK),
                          gla_onorm_g[l])
        qb = rms_norm_2(qb.reshape(Bsz, S, DIL_HEADS, DIL_DH), q_norm_g[l])
        kb = rms_norm_2(kb.reshape(Bsz, S, DIL_HEADS, DIL_DH), k_norm_g[l])
        out_b = dilated_mixer(qb, kb, vb.reshape(Bsz, S, DIL_HEADS, DIL_DH), rel_bias)
        mix = jnp.concatenate([out_a.astype(x.dtype), out_b.astype(x.dtype)], axis=-1)
        x = x + mix @ w_out[l]
        h2 = rms_norm_2(x, norm2_g[l])
        x = x + (jax.nn.silu(h2 @ w_gate[l]) * (h2 @ w_up[l])) @ w_down[l]
    return x


def setup_inputs(seed=0):
    out = dict(first_inputs(seed))
    for name, value in second_inputs(seed + 1).items():
        if name != "x":
            out[name + "_2"] = value
    return out


def reference(
    x, positions, mix_norm, ffn_norm, fox_w_in, fox_b_f, fox_q_gain, fox_k_gain, fox_w_out,
    mla_w_in, mla_q_a_gain, mla_kv_a_gain, mla_w_q_b, mla_w_kv_b, mla_q_gain, mla_k_gain,
    mla_w_out, sb_w_in, sb_q_gain, sb_k_gain, sb_w_out, sgu_w_in, sgu_v_gain, sgu_w_s, sgu_b_s,
    sgu_w_out, ffn_w_up, ffn_conv_w, ffn_conv_b, ffn_w_down, norm1_g_2, w_in_2, gla_gate_w2_2,
    gla_gate_b_2, gla_onorm_g_2, q_norm_g_2, k_norm_g_2, rel_bias_2, w_out_2, norm2_g_2,
    w_gate_2, w_up_2, w_down_2,
):
    x = first_block(
        x, positions, mix_norm, ffn_norm, fox_w_in, fox_b_f, fox_q_gain, fox_k_gain, fox_w_out,
        mla_w_in, mla_q_a_gain, mla_kv_a_gain, mla_w_q_b, mla_w_kv_b, mla_q_gain, mla_k_gain,
        mla_w_out, sb_w_in, sb_q_gain, sb_k_gain, sb_w_out, sgu_w_in, sgu_v_gain, sgu_w_s,
        sgu_b_s, sgu_w_out, ffn_w_up, ffn_conv_w, ffn_conv_b, ffn_w_down,
    )
    return second_block(
        x, norm1_g_2, w_in_2, gla_gate_w2_2, gla_gate_b_2, gla_onorm_g_2, q_norm_g_2,
        k_norm_g_2, rel_bias_2, w_out_2, norm2_g_2, w_gate_2, w_up_2, w_down_2,
    )


_drawn_inputs = setup_inputs


def setup_inputs(seed=0):
    import zlib

    import numpy as np

    out = dict(_drawn_inputs(seed))
    spreads = {}
    factors = {'ffn_conv_b': 6.395,
     'norm1_g_2': 3.772,
     'gla_gate_b_2': 3.881,
     'gla_onorm_g_2': 8.0,
     'q_norm_g_2': 8.0,
     'k_norm_g_2': 8.0,
     'norm2_g_2': 12.734,
     'rel_bias_2': 5.687}
    for name, (base, spread) in spreads.items():
        noise = np.random.default_rng([zlib.crc32(name.encode()), seed]).standard_normal(out[name].shape)
        drawn = base * np.exp(spread * noise) if base else spread * noise
        out[name] = __import__('jax').numpy.asarray(drawn.astype(out[name].dtype))
    for name, factor in factors.items():
        out[name] = (out[name] * factor).astype(out[name].dtype)
    return out
```

```python
from contextlib import ExitStack

import numpy as np

import concourse.bass as bass
from concourse import mybir

F32 = mybir.dt.float32
F32R = mybir.dt.float32r
BF16 = mybir.dt.bfloat16
I32 = mybir.dt.int32
ALU = mybir.AluOpType
ACT = mybir.ActivationFunctionType
AX_X = mybir.AxisListType.X

P = 128
S = 256
D = 2048
KC = D // P
FF = 5632
FC = FF // P
EPS = 1e-6
BLOCKS = 8
UW = BLOCKS * P
RING = 4
AHEAD = 3
XQ = KC // RING

FOX_HEADS = 16
GLA_HEADS = 4
DIL_HEADS = 8
GLA_DV = 256
GLA_CHUNK = 64
GLA_TAU = 16.0
HEAD_UNITS = 6
GLA_UNITS = 12
REL_BUCKETS = 32
REL_MAX_DIST = 2048
DIL_PATTERNS = ((128, 1), (512, 4), (2048, 16))
NEG_INF = -1e30
TOEPLITZ = 384

IN_CHUNKS = 49
U_IN = 2 * IN_CHUNKS
U_OUT = 2 * KC
U_UP = 4 * FC
U_DOWN = KC * FC // BLOCKS
U_LAYER = U_IN + U_OUT + U_UP + U_DOWN
UNITS = 2 * U_LAYER
C_LAYER = IN_CHUNKS + KC + 2 * FC + KC

COL = {}
for _name, _n in (("norm0", KC), ("norm1", KC), ("norm2", KC), ("norm3", KC), ("conv0", 2 * FC), ("conv1", 2 * FC),
                  ("conv2", 2 * FC), ("convb", 2 * FC), ("fox_q", 1), ("fox_k", 1), ("dil_q", 1), ("dil_k", 1),
                  ("onorm", GLA_DV // P), ("gate_b", GLA_HEADS), ("fox_b", 1)):
    COL[_name] = (sum(n for _, n in COL.values()), _n)
VECTORS = sum(n for _, n in COL.values())


class Pos:

    def __init__(self, base, per=0, i=0):
        self.base, self.per, self.i = base, per, i

    def unit(self, k):
        return self.base + k + self.per * self.i

    def slot(self, k):
        return (self.base + k) % RING

    def lap(self, k):
        return (self.base + k) // RING + self.per // RING * self.i


def build(nc, wstream, xt, vectors, identity, dist_onehot, rel_bias, gate_w2, scan_keep, gla_mask, fox_mask, out):
    with ExitStack() as ctx:
        def sb(name, shape, dt=F32):
            return ctx.enter_context(nc.sbuf_tensor(name, shape, dt))

        def sem(name):
            return ctx.enter_context(nc.semaphore(name))

        raw = [sb(f"raw{i}", [P, UW]) for i in range(RING)]
        whi = [sb(f"whi{i}", [P, UW], F32R) for i in range(RING)]
        wlo = [sb(f"wlo{i}", [P, UW], F32R) for i in range(RING)]
        xres = sb("xres", [P, KC, S])
        xs_hi = sb("xs_hi", [P, KC, S], F32R)
        xs_lo = sb("xs_lo", [P, KC, S], F32R)
        vec = sb("vec", [P, VECTORS])
        ident = sb("ident", [P, P])
        ident_bf = sb("ident_bf", [P, P], BF16)
        maskneg_bf = sb("maskneg_bf", [P, P], BF16)
        mean_d = sb("mean_d", [P, P])
        mean_h = sb("mean_h", [P, P])
        eps = sb("eps", [P, 1])
        qk_gain = sb("qk_gain", [P, 4])
        sq_x = sb("sq_x", [P, 2, S])
        sq_sum = sb("sq_sum", [P, S])
        ln_x = sb("ln_x", [P, S])
        rstd = sb("rstd", [P, S])
        up_g = sb("up_g", [P, S + 2])
        up_v = sb("up_v", [P, S + 2])
        tap_g = sb("tap_g", [P, S])
        tap_v = sb("tap_v", [P, S])
        silu_g = sb("silu_g", [P, S])
        hid = sb("hid", [P, S])

        arena = nc.sbuf_base

        def place(start):
            at = [start]

            def put(name, shape, dt=F32):
                t = nc.alloc_sbuf_tensor_at(name, shape, dt, offset=at[0])
                at[0] += int(np.prod(shape[1:])) * 4
                assert at[0] <= nc.sbuf_usable_end, (name, at[0])
                return t
            return put, at

        put, _ = place(arena)
        hid_hi = put("hid_hi", [P, FC, S], F32R)
        hid_lo = put("hid_lo", [P, FC, S], F32R)
        put, at_att = place(arena)
        mix_hi = put("mix_hi", [P, KC, S], F32R)
        mix_lo = put("mix_lo", [P, KC, S], F32R)
        at_tables = at_att[0]
        decay_row = put("decay_row", [P, FOX_HEADS, S])
        qk = put("qk", [P, 2, S])
        qk_n = put("qk_n", [P, 2, S])
        sq_qk = put("sq_qk", [P, 2, S])
        ln_qk = put("ln_qk", [P, 2, S])
        rstd_qk = put("rstd_qk", [P, 2, S])
        v_t = put("v_t", [P, S])
        v_tok = put("v_tok", [P, 2, P])
        biased = put("biased", [P, 3 * P])
        probs = put("probs", [P, 3 * P])
        probs_t = put("probs_t", [P, 3 * P])
        head_o = put("head_o", [P, S])
        stat = put("stat", [P, 2, 4])
        at_gla = at_att[0]
        put, _ = place(at_gla)
        f_z, f_negabs, f_exp, f_ln, f_neg, f_cum, f_one = (put(f"f_{i}", [P, S]) for i in range(7))
        mask_sb = put("mask_sb", [P, P])
        dist_sb = put("dist_sb", [REL_BUCKETS + 1, TOEPLITZ])
        rel_sb = put("rel_sb", [REL_BUCKETS + 1, DIL_HEADS])
        dist_bias = put("dist_bias", [DIL_HEADS, TOEPLITZ])
        put, at_tab = place(at_tables)
        toeplitz = put("toeplitz", [P, DIL_HEADS, S])
        eb = put("eb", [P, GLA_HEADS, S])
        enb = put("enb", [P, GLA_HEADS, S])
        assert at_tab[0] <= at_tables + FOX_HEADS * S * 4
        put, _ = place(at_gla)
        g_q, g_k = put("g_q", [P, S]), put("g_k", [P, S])
        g_qt, g_kt, g_kd = put("g_qt", [P, S]), put("g_kt", [P, S]), put("g_kd", [P, S])
        g_v = put("g_v", [P, 2, S])
        g_vtok = put("g_vtok", [P, 2, GLA_DV])
        g_kdtok = put("g_kdtok", [P, 2, P])
        g_attn = put("g_attn", [P, 2, GLA_CHUNK])
        g_r = put("g_r", [P, 2, S])
        g_silu = put("g_silu", [P, 2, S])
        g_state = put("g_state", [P, 3, GLA_DV])
        g_on = put("g_on", [P, 2, GLA_DV])
        g_of = put("g_of", [P, 2, S])
        g_stat = put("g_stat", [P, 2, 4])
        g_mask = put("g_mask", [P, GLA_CHUNK], I32)
        w2_sb = put("w2_sb", [16, GLA_HEADS * P])
        put, at_z = place(at_tables + FOX_HEADS * S * 4)
        ga = put("ga", [16, S])
        g_keep = put("g_keep", [P, S])
        g_z = put("g_z", [P, GLA_HEADS, S])
        g_t = put("g_t", [P, GLA_HEADS, S])
        g_l = put("g_l", [P, GLA_HEADS, S])
        assert at_z[0] <= at_gla

        dist_dram = nc.dram_tensor("dist_scratch", [DIL_HEADS, P, TOEPLITZ], F32)
        decay_dram = nc.dram_tensor("decay_scratch", [FOX_HEADS, S], F32)

        def bank(name):
            return ctx.enter_context(nc.psum_tensor(name, [P, 512], F32))

        acc = [bank(f"acc{i}") for i in range(4)]
        b_mean, b_score, b_turn, b_val = bank("b_mean"), bank("b_score"), bank("b_turn"), bank("b_val")

        raw_landed = [sem(f"raw_landed{i}") for i in range(RING)]
        hi_ready, lo_ready, unit_used = sem("hi_ready"), sem("lo_ready"), sem("unit_used")
        chunk_out = sem("chunk_out")
        x_landed = [sem(f"x_landed{i}") for i in range(RING)]
        vec_landed, consts_landed, tables_landed, toeplitz_landed = (sem("vec_landed"), sem("consts_landed"), sem("tables_landed"),
                                                                     sem("toeplitz_landed"))
        setup_done, bias_made, bias_out, bias_stored = sem("setup_done"), sem("bias_made"), sem("bias_out"), sem("bias_stored")
        xs_hi_ready, xs_ready, sq_ready, sumsq = sem("xs_hi_ready"), sem("xs_ready"), sem("sq_ready"), sem("sumsq")
        mean_ready, ln_ready, rstd_ready = sem("mean_ready"), sem("ln_ready"), sem("rstd_ready")
        f_step, f_act, decay_out, decay_stored, decay_landed = (sem("f_step"), sem("f_act"), sem("decay_out"),
                                                                sem("decay_stored"), sem("decay_landed"))
        qk_sq, qk_mean, qk_ln, qk_rstd, qk_scaled, qk_ready = (sem("qk_sq"), sem("qk_mean"), sem("qk_ln"), sem("qk_rstd"),
                                                               sem("qk_scaled"), sem("qk_ready"))
        v_turned, v_ready, scores_ready = sem("v_turned"), sem("v_ready"), sem("scores_ready")
        bias_added, row_max, neg_max, exp_ready, row_inv, probs_ready = (
            sem("bias_added"), sem("row_max"), sem("neg_max"), sem("exp_ready"), sem("row_inv"), sem("probs_ready"))
        probs_turned, probs_t_ready, head_ready = sem("probs_turned"), sem("probs_t_ready"), sem("head_ready")
        head_copied, mix_hi_ready, mix_ready = sem("head_copied"), sem("mix_hi_ready"), sem("mix_ready")
        gate_pre, gate_step, gate_act, gate_ready = sem("gate_pre"), sem("gate_step"), sem("gate_act"), sem("gate_ready")
        g_qk_ready, g_intra, g_intra_ready, g_kd_ready = sem("g_qk_ready"), sem("g_intra"), sem("g_intra_ready"), sem("g_kd_ready")
        g_vturned, g_v_ready, g_cs, g_states, g_out = sem("g_vturned"), sem("g_v_ready"), sem("g_cs"), sem("g_states"), sem("g_out")
        g_ss, g_lns, g_rstd, g_on_ready, g_turned = sem("g_ss"), sem("g_lns"), sem("g_rstd"), sem("g_on_ready"), sem("g_turned")
        g_silu_ready, g_gated, g_hi, g_mixed = sem("g_silu_ready"), sem("g_gated"), sem("g_hi"), sem("g_mixed")
        tap0, taps, gate_val, silu_ready, hid_ready, hid_hi_ready, hid_split = (
            sem("tap0"), sem("taps"), sem("gate_val"), sem("silu_ready"), sem("hid_ready"), sem("hid_hi_ready"), sem("hid_split"))
        out_stored = sem("out_stored")

        def column(name, c=0):
            return vec[:, bass.ds(COL[name][0] + c, 1)]

        class Layer:
            def __init__(self, n):
                self.n = n
                self.unit_in = U_LAYER * n
                self.unit_heads = self.unit_in + 2
                self.unit_out = self.unit_in + U_IN
                self.unit_up = self.unit_out + U_OUT
                self.unit_down = self.unit_up + U_UP
                self.chunk_in = C_LAYER * n
                self.chunk_heads = self.chunk_in + 1
                self.chunk_out = self.chunk_in + IN_CHUNKS
                self.chunk_up = self.chunk_out + KC
                self.chunk_down = self.chunk_up + 2 * FC

        L0, L1 = Layer(0), Layer(1)
        UNIT_DIL = L1.unit_heads + GLA_HEADS * GLA_UNITS
        CHUNK_DIL = L1.chunk_heads + GLA_HEADS * 6

        class Heads:

            def __init__(self, kind, n, unit0, chunk0, count0, mix0):
                self.kind, self.n, self.unit0, self.chunk0, self.count0, self.mix0 = kind, n, unit0, chunk0, count0, mix0

            def pos(self, i):
                return Pos(self.unit0, 2 * HEAD_UNITS, i)

        FOX = Heads("fox", FOX_HEADS, L0.unit_heads, L0.chunk_heads, 0, 0)
        DIL = Heads("dil", DIL_HEADS, UNIT_DIL, CHUNK_DIL, FOX_HEADS, 2 * GLA_HEADS)
        block = ctx.enter_context(nc.Block())

        @block.sync
        def _(sp):
            def load(u, slot):
                sp.dma_start(raw[slot][:, :], wstream[u, :, :]).then_inc(raw_landed[slot], 16)

            for u in range(RING):
                c = slice(XQ * u, XQ * (u + 1))
                sp.dma_start(xres[:, c, :], xt[:, c, :]).then_inc(x_landed[u], 16)
                load(u, u)
            with sp.Fori(1, UNITS // RING) as lap:
                for slot in range(RING):
                    sp.wait_ge(lo_ready, RING * lap + slot - RING + 1)
                    load(RING * lap + slot, slot)
            sp.wait_ge(out_stored, 16 * KC)

        @block.gpsimd
        def _(pool):
            def bring(dst, src, done):
                pool.dma_start(dst, src).then_inc(done, 16)

            bring(ident[:, :], identity, consts_landed)
            bring(mask_sb[:, :], fox_mask, consts_landed)
            bring(dist_sb[:, :], dist_onehot, consts_landed)
            bring(rel_sb[0:REL_BUCKETS, :], rel_bias, consts_landed)
            pool.wait_ge(decay_out, 1)
            bring(decay_dram[:, :], f_cum[0:FOX_HEADS, :], decay_stored)
            pool.wait_ge(decay_stored, 16)
            bring(decay_row[:, :, :], bass.AP(decay_dram, 0, [[0, P], [S, FOX_HEADS], [1, S]]), decay_landed)
            pool.wait_ge(bias_out, 1)
            bring(dist_dram[:, :, :], dist_bias[:, :].rearrange("h (a w) -> h a w", a=1).to_broadcast([DIL_HEADS, P, TOEPLITZ]),
                  bias_stored)
            pool.wait_ge(bias_stored, 16)
            pool.wait_ge(unit_used, L1.unit_in)
            bring(w2_sb[:, :], gate_w2, tables_landed)
            bring(g_mask[:, :], gla_mask, tables_landed)
            bring(g_keep[:, :], scan_keep, tables_landed)
            for h in range(DIL_HEADS):
                bring(toeplitz[:, h, :], bass.AP(dist_dram, (h * P * TOEPLITZ) + P - 1, [[TOEPLITZ - 1, P], [1, S]]), toeplitz_landed)

        @block.tensor
        def _(pe):
            def unit(pos, k, blocks, x_hi, x_lo):
                slot = pos.slot(k)
                pe.wait_ge(lo_ready, pos.unit(k) + 1)
                for j, (bank_no, kc, first, last, late) in enumerate(blocks):
                    if late:
                        pe.wait_ge(*late)
                    w_hi = whi[slot][:, j * P:(j + 1) * P]
                    w_lo = wlo[slot][:, j * P:(j + 1) * P]
                    o = acc[bank_no][:, 0:S]
                    pe.matmul(o, w_hi, x_hi[:, kc, :], start=first, stop=False)
                    pe.matmul(o, w_hi, x_lo[:, kc, :], start=False, stop=False)
                    mm = pe.matmul(o, w_lo, x_hi[:, kc, :], start=False, stop=last)
                mm.then_inc(unit_used, 1)

            def half(pos, k, bank_no, part, x_hi, x_lo, late=None):
                late = late or {}
                unit(pos, k, [(bank_no, 8 * part + j, part == 0 and j == 0, part == 1 and j == 7, late.get(8 * part + j))
                              for j in range(BLOCKS)], x_hi, x_lo)

            def whole(pos, k, bank_no, chunk):
                pe.wait_ge(chunk_out, chunk - 2)
                half(pos, k, bank_no, 0, xs_hi, xs_lo)
                half(pos, k + 1, bank_no, 1, xs_hi, xs_lo)

            def norm_mean(n):
                pe.wait_ge(sumsq, KC * (n + 1))
                if n % 2:
                    pe.wait_ge(head_copied, FOX_HEADS + n // 2 * DIL_HEADS)
                elif n:
                    pe.wait_ge(rstd_ready, n)
                pe.matmul(b_mean[:, 0:S], mean_d[:, :], sq_sum[:, :], start=True, stop=True).then_inc(mean_ready, 1)

            def head_mean(h):
                pe.wait_ge(qk_sq, 2 * h + 2)
                pe.matmul(b_mean[:, :], mean_h[:, :], sq_qk[:, :, :].rearrange("p a s -> p (a s)"),
                          start=True, stop=True).then_inc(qk_mean, 1)

            def head_scores(h, kind):
                pe.wait_ge(qk_ready, 2 * h + 2)
                for t in range(2):
                    mm = pe.transpose(b_val[:, t * P:(t + 1) * P], v_t[:, t * P:(t + 1) * P], ident[:, :])
                mm.then_inc(v_turned, 1)
                if kind == "fox":
                    pe.matmul(b_score[:, 0:P], ident_bf[:, :], maskneg_bf[:, :], start=True, stop=False)
                pe.matmul(b_score[:, 0:P], qk_n[:, 0, 0:P], qk_n[:, 1, 0:P], start=kind != "fox", stop=True)
                mm = pe.matmul(b_score[:, P:3 * P], qk_n[:, 0, P:S], qk_n[:, 1, :], start=True, stop=kind != "fox")
                if kind == "fox":
                    mm = pe.matmul(b_score[:, 2 * P:3 * P], ident_bf[:, :], maskneg_bf[:, :], start=False, stop=True)
                mm.then_inc(scores_ready, 1)

            def head_turn(h):
                pe.wait_ge(probs_ready, 2 * h + 2)
                for part, col in ((0, 0), (1, P), (2, 2 * P)):
                    mm = pe.transpose(b_turn[:, col:col + P], probs[:, part * P:(part + 1) * P], ident[:, :])
                mm.then_inc(probs_turned, 1)

            def head_values(h, means):
                pe.wait_ge(probs_t_ready, h + 1)
                pe.wait_ge(qk_rstd, means)
                pe.matmul(b_mean[:, 0:P], v_tok[:, 0, :], probs_t[:, 0:P], start=True, stop=True)
                pe.matmul(b_mean[:, P:S], v_tok[:, 0, :], probs_t[:, P:S], start=True, stop=False)
                pe.matmul(b_mean[:, P:S], v_tok[:, 1, :], probs_t[:, S:3 * P], start=False, stop=True).then_inc(head_ready, 1)

            def head(run, pos, h, k0, lag):
                n = run.count0 + h
                chunk = run.chunk0 + 3 * h
                whole_q = lambda part: half(pos, k0 + part, 1, part, xs_hi, xs_lo)
                pe.wait_ge(chunk_out, chunk - 2)
                whole_q(0)
                whole_q(1)
                if lag >= 2:
                    head_values(n - 2, n)
                if lag >= 1:
                    head_scores(n - 1, run.kind)
                whole(pos, k0 + 2, 2, chunk + 1)
                pe.wait_ge(chunk_out, chunk)
                half(pos, k0 + 4, 3, 0, xs_hi, xs_lo)
                if lag >= 1:
                    head_turn(n - 1)
                half(pos, k0 + 5, 3, 1, xs_hi, xs_lo)
                if lag >= 2:
                    pe.wait_ge(head_copied, n - 1)
                head_mean(n)

            def gla_intra(g):
                pe.wait_ge(g_qk_ready, g + 1)
                for n in range(4):
                    r = GLA_CHUNK * (n % 2)
                    c = slice(GLA_CHUNK * n, GLA_CHUNK * (n + 1))
                    mm = pe.matmul(b_score[r:r + GLA_CHUNK, GLA_CHUNK * (n // 2):GLA_CHUNK * (n // 2 + 1)],
                                   g_kt[:, c], g_qt[:, c], start=True, stop=True)
                for t in range(2):
                    mm = pe.transpose(b_turn[:, t * P:(t + 1) * P], g_kd[:, t * P:(t + 1) * P], ident[:, :])
                mm.then_inc(g_intra, 1)

            def gla_turn_v(g, lag):
                pe.wait_ge(chunk_out, L1.chunk_heads + 6 * g + 4)
                if lag:
                    pe.wait_ge(g_gated, g)
                for t in range(2):
                    for c in range(2):
                        mm = pe.transpose(b_val[:, t * GLA_DV + c * P:t * GLA_DV + (c + 1) * P],
                                          g_v[:, c, t * P:(t + 1) * P], ident[:, :])
                mm.then_inc(g_vturned, 1)

            def gla_chunk_states(g):
                pe.wait_ge(g_v_ready, g + 1)
                pe.wait_ge(g_kd_ready, g + 1)
                pe.wait_ge(g_intra_ready, g + 1)
                for n in range(3):
                    r = GLA_CHUNK * (n % 2)
                    o = b_turn[:, 0:GLA_DV] if n == 1 else b_score[:, GLA_DV * (n // 2):GLA_DV * (n // 2 + 1)]
                    mm = pe.matmul(o, g_kdtok[r:r + GLA_CHUNK, n // 2, :], g_vtok[r:r + GLA_CHUNK, n // 2, :],
                                   start=True, stop=True)
                mm.then_inc(g_cs, 1)

            def gla_outputs(g):
                pe.wait_ge(g_states, 3 * g + 3)
                for n in (1, 2, 3, 0):
                    r = GLA_CHUNK * (n % 2)
                    rows = slice(r, r + GLA_CHUNK)
                    o = b_mean[rows, GLA_DV * (n // 2):GLA_DV * (n // 2 + 1)]
                    if n:
                        pe.matmul(o, g_qt[:, GLA_CHUNK * n:GLA_CHUNK * (n + 1)], g_state[:, n - 1, :], start=True, stop=False)
                    mm = pe.matmul(o, g_attn[rows, n // 2, :], g_vtok[rows, n // 2, :], start=n == 0, stop=True)
                mm.then_inc(g_out, 1)

            def gla_turn_out(g):
                pe.wait_ge(g_on_ready, 2 * g + 2)
                for c in range(2):
                    for t in range(2):
                        mm = pe.transpose(b_val[:, c * S + t * P:c * S + (t + 1) * P], g_on[:, t, c * P:(c + 1) * P], ident[:, :])
                mm.then_inc(g_turned, 1)

            def gla_head(g, pos):
                chunk = L1.chunk_heads + 6 * g
                after = {0: lambda: gla_outputs(g - 1), 2: lambda: gla_turn_out(g - 1),
                         7: lambda: gla_intra(g), 9: lambda: gla_turn_v(g, True), 10: lambda: gla_chunk_states(g)}
                for c in range(6):
                    pe.wait_ge(chunk_out, chunk + c - 2)
                    for part in range(2):
                        half(pos, 2 * c + part, 1 + c % 3, part, xs_hi, xs_lo)
                        after.get(2 * c + part, lambda: None)()

            def project(layer, run):
                last = run.count0 + run.n - 1
                between = {0: (lambda: head_values(last - 1, last + 1), lambda: head_scores(last, run.kind)),
                           2: (lambda: head_turn(last),), 3: (lambda: pe.wait_ge(head_copied, last), lambda: head_values(last, last + 1))}

                def group(pos, i, tail):
                    for part in range(2):
                        for c in range(4):
                            if part == 0:
                                pe.wait_ge(chunk_out, layer.chunk_out + 4 * i + c - 3)
                            late = {}
                            if tail and part == 0 and c == 0:
                                late = {0: (mix_ready, run.count0 + run.n - 2)}
                                if layer.n:
                                    pe.wait_ge(g_mixed, GLA_HEADS)
                            if tail and part == 1 and c == 0:
                                late = {KC - 2: (mix_ready, run.count0 + run.n - 1), KC - 1: (mix_ready, run.count0 + run.n)}
                            half(pos, 4 * part + c, c, part, mix_hi, mix_lo, late)
                            if tail:
                                for piece in between.get(4 * part + c, ()):
                                    piece()

                group(Pos(layer.unit_out), 0, True)
                with pe.Fori(1, KC // 4) as i:
                    group(Pos(layer.unit_out, 8, i), i, False)

            def up(layer):
                norm = 2 * layer.n + 1

                def pairs(pos, i, first):
                    for j in range(2):
                        for part in range(2):
                            for c in range(2):
                                if part == 0:
                                    pe.wait_ge(chunk_out, layer.chunk_up + 4 * i + 2 * j + c - 3)
                                late = {}
                                if first and j == 0 and c == 0:
                                    late = {8 * part + m: (xs_ready, KC * norm + 8 * part + m + 1) for m in (0, 7)}
                                    if part == 0:
                                        late = {0: (xs_ready, KC * norm + 8)}
                                half(pos, 4 * j + 2 * part + c, 2 * j + c, part, xs_hi, xs_lo, late)
                                if first and j == 0 and part == 0 and c == 1:
                                    norm_mean(norm)

                pairs(Pos(layer.unit_up), 0, True)
                with pe.Fori(1, FC // 2) as i:
                    pairs(Pos(layer.unit_up, 8, i), i, False)

            def down(layer):
                with pe.Fori(0, 2) as i:
                    pos = Pos(layer.unit_down, U_DOWN // 2, i)
                    pe.wait_ge(hid_split, FC * (layer.n + 1) - 1)
                    for k in range(U_DOWN // 2):
                        blocks = []
                        for b in range(BLOCKS * k, BLOCKS * (k + 1)):
                            c, kc = divmod(b, FC)
                            if kc == 0:
                                pe.wait_ge(chunk_out, layer.chunk_down + 8 * i + c - 3)
                            late = (hid_split, FC * (layer.n + 1)) if b == FC - 1 else None
                            blocks.append((c % 4, kc, kc == 0, kc == FC - 1, late))
                        unit(pos, k, blocks, hid_hi, hid_lo)

            for part in range(2):
                half(Pos(0), part, 0, part, xs_hi, xs_lo, {8 * part + j: (xs_ready, 8 * part + j + 1) for j in range(BLOCKS)})

            def distance_biases():
                pe.wait_ge(consts_landed, 16 * 4)
                pe.wait_ge(setup_done, 1)
                pe.matmul(b_score[0:DIL_HEADS, 0:TOEPLITZ], rel_sb[:, :], dist_sb[:, :], start=True, stop=True).then_inc(bias_made, 1)

            for j in range(2):
                chunk = FOX.chunk0 + 3 * j
                for c, (k, bank_no) in enumerate(((0, 1), (2, 2), (4, 3))):
                    if chunk + c - 2 >= 1:
                        pe.wait_ge(chunk_out, chunk + c - 2)
                    half(Pos(L0.unit_heads), HEAD_UNITS * j + k, bank_no, 0, xs_hi, xs_lo)
                    if c == 1 and not j:
                        norm_mean(0)
                        distance_biases()
                    if c == 2 and j:
                        head_turn(j - 1)
                    half(Pos(L0.unit_heads), HEAD_UNITS * j + k + 1, bank_no, 1, xs_hi, xs_lo)
                    if c == 0 and j:
                        pe.wait_ge(setup_done, 2)
                        head_scores(j - 1, "fox")
                pe.wait_ge(qk_rstd, j) if j else pe.wait_ge(rstd_ready, 1)
                head_mean(j)
            with pe.Fori(1, FOX_HEADS // 2) as i:
                for j in range(2):
                    head(FOX, FOX.pos(i), 2 * i + j, HEAD_UNITS * j, 2)
            project(L0, FOX)
            up(L0)
            down(L0)

            pe.wait_ge(chunk_out, L1.chunk_in - 3)
            for part in range(2):
                half(Pos(L1.unit_in), part, 0, part, xs_hi, xs_lo,
                     {8 * part: (xs_ready, 2 * KC + 8 * (part + 1) - 1), 8 * part + 7: (xs_ready, 2 * KC + 8 * (part + 1))})
            norm_mean(2)

            def gates():
                pe.wait_ge(tables_landed, 16 * 3)
                pe.wait_ge(chunk_out, L1.chunk_in + 1)
                for g in range(GLA_HEADS):
                    o = (b_score, b_turn)[g // 2][:, (g % 2) * S:(g % 2 + 1) * S]
                    mm = pe.matmul(o, w2_sb[:, g * P:(g + 1) * P], ga[:, :], start=True, stop=True)
                mm.then_inc(gate_pre, 1)

            for c in range(6):
                pe.wait_ge(chunk_out, L1.chunk_heads + c - 2)
                for part in range(2):
                    k = 2 * c + part
                    half(Pos(L1.unit_heads), k, 1 + c % 3, part, xs_hi, xs_lo)
                    if k == 2:
                        gates()
                    if k == 7:
                        gla_intra(0)
                    if k == 9:
                        gla_turn_v(0, False)
                    if k == 10:
                        gla_chunk_states(0)
            with pe.Fori(1, GLA_HEADS) as g:
                gla_head(g, Pos(L1.unit_heads, GLA_UNITS, g))
            for j in range(2):
                chunk = DIL.chunk0 + 3 * j
                n = DIL.count0 + j
                for c in range(3):
                    pe.wait_ge(chunk_out, chunk + c - 2)
                    for part in range(2):
                        k = 2 * c + part
                        half(Pos(DIL.unit0), HEAD_UNITS * j + k, 1 + c, part, xs_hi, xs_lo)
                        if not j and k == 0:
                            gla_outputs(GLA_HEADS - 1)
                        if not j and k == 2:
                            gla_turn_out(GLA_HEADS - 1)
                        if j and k == 1:
                            head_scores(n - 1, "dil")
                        if j and k == 4:
                            head_turn(n - 1)
                pe.wait_ge(qk_rstd, n) if j else pe.wait_ge(g_on_ready, 2 * GLA_HEADS)
                head_mean(n)
            with pe.Fori(1, DIL_HEADS // 2) as i:
                for j in range(2):
                    head(DIL, DIL.pos(i), 2 * i + j, HEAD_UNITS * j, 2)
            project(L1, DIL)
            up(L1)
            down(L1)

        @block.scalar
        def _(act):
            def split_hi(pos, k):
                k += AHEAD
                slot = pos.slot(k)
                act.wait_ge(raw_landed[slot], 16 * pos.lap(k) + 16)
                if pos.per or pos.base + k >= RING:
                    act.wait_ge(unit_used, pos.unit(k) - RING + 1)
                act.activation(whi[slot][:, :], raw[slot][:, :], ACT.Copy).then_inc(hi_ready, 1)

            def residual(n, c, chunk):
                act.wait_ge(chunk_out, chunk + 1)
                act.activation(xs_hi[:, c, :], xres[:, c, :], ACT.Copy, scale=column(f"norm{n}", c)).then_inc(xs_hi_ready, 1)
                act.activation(sq_x[:, slot2(c), :], xres[:, c, :], ACT.Square).then_inc(sq_ready, 1)

            def slot2(c):
                return c % 2 if isinstance(c, int) else c.static % 2

            def norm_rstd(n):
                act.wait_ge(mean_ready, n + 1)
                act.activation(ln_x[:, :], b_mean[:, 0:S], ACT.Ln, bias=eps[:, :]).then_inc(ln_ready, 1)
                act.wait_ge(ln_ready, n + 1)
                act.activation(rstd[:, :], ln_x[:, :], ACT.Exp, scale=-0.5).then_inc(rstd_ready, 1)

            def square(n, which, chunk):
                act.wait_ge(chunk_out, chunk + 1)
                act.activation(sq_qk[:, which, :], qk[:, which, :], ACT.Square).then_inc(qk_sq, 1)

            def head_rstd(n):
                act.wait_ge(qk_mean, n + 1)
                act.activation(ln_qk[:, :, :].rearrange("p a s -> p (a s)"), b_mean[:, :], ACT.Ln, bias=eps[:, :]).then_inc(qk_ln, 1)
                act.wait_ge(qk_ln, n + 1)
                act.activation(rstd_qk[:, :, :], ln_qk[:, :, :], ACT.Exp, scale=-0.5).then_inc(qk_rstd, 1)

            def copy_v(n):
                act.wait_ge(v_turned, n + 1)
                act.activation(v_tok[:, :, :].rearrange("p a s -> p (a s)"), b_val[:, 0:S], ACT.Copy).then_inc(v_ready, 1)

            def exps(n):
                for t, (a, b) in enumerate(((0, P), (P, 3 * P))):
                    act.wait_ge(neg_max, 2 * n + t + 1)
                    act.activation(probs[:, a:b], biased[:, a:b], ACT.Exp, bias=stat[:, t, 1:2],
                                   accum_out=stat[:, t, 2:3]).then_inc(exp_ready, 1)

            def copy_probs_t(n):
                act.wait_ge(probs_turned, n + 1)
                act.activation(probs_t[:, :], b_turn[:, 0:3 * P], ACT.Copy).then_inc(probs_t_ready, 1)

            def head_hi(n, at):
                act.wait_ge(head_copied, n + 1)
                act.activation(mix_hi[:, at, :], head_o[:, :], ACT.Copy).then_inc(mix_hi_ready, 1)

            def head_step(run, n, at, s, chunk, lag, own=True):
                if s == 2 and lag >= 2:
                    head_hi(n - 2, at - 2)
                if s == 2 and own:
                    square(n, 0, chunk)
                if s == 2 and lag >= 1:
                    copy_v(n - 1)
                    exps(n - 1)
                if s == 4 and own:
                    square(n, 1, chunk + 1)
                if s == 5 and lag >= 1:
                    copy_probs_t(n - 1)

            def tail_step(run, s):
                n = run.count0 + run.n
                at = run.mix0 + run.n
                if s == 1:
                    head_hi(n - 2, at - 2)
                    copy_v(n - 1)
                    exps(n - 1)
                if s == 3:
                    copy_probs_t(n - 1)
                if s == 4:
                    head_hi(n - 1, at - 1)

            def gla_step(g, s, chunk, lag, own=True):
                if s == 1 and lag:
                    act.wait_ge(g_out, g)
                    for t in range(2):
                        act.activation(g_of[:, t, :], b_mean[:, t * GLA_DV:(t + 1) * GLA_DV], ACT.Square,
                                       accum_out=g_stat[:, t, 0:1]).then_inc(g_ss, 1)
                    act.wait_ge(g_ss, 2 * g)
                    act.activation(g_stat[:, :, 1], g_stat[:, :, 0], ACT.Ln, bias=eps[:, :], scale=1.0 / GLA_DV).then_inc(g_lns, 1)
                    act.wait_ge(g_lns, g)
                    act.activation(g_stat[:, :, 2], g_stat[:, :, 1], ACT.Exp, scale=-0.5).then_inc(g_rstd, 1)
                    act.wait_ge(chunk_out, chunk)
                    act.activation(g_silu[:, :, :], g_r[:, :, :], ACT.Silu).then_inc(g_silu_ready, 1)
                if s == 3 and lag:
                    act.wait_ge(g_gated, g)
                    act.activation(mix_hi[:, bass.ds(2 * g - 2, 2), :], g_of[:, :, :], ACT.Copy).then_inc(g_hi, 1)
                if s == 8 and own:
                    act.wait_ge(g_intra, g + 1)
                    act.activation(g_kdtok[:, :, :].rearrange("p a s -> p (a s)"), b_turn[:, 0:S], ACT.Copy).then_inc(g_kd_ready, 1)
                if s == 10 and own:
                    act.wait_ge(g_vturned, g + 1)
                    act.activation(g_vtok[:, :, :].rearrange("p a s -> p (a s)"), b_val[:, :], ACT.Copy).then_inc(g_v_ready, 1)

            def tap_gate(layer, j, chunk):
                act.wait_ge(chunk_out, chunk + 1)
                if layer.n == 0:
                    act.activation(tap_g[:, :], up_g[:, 0:S], ACT.Identity, scale=column("conv0", j),
                                   bias=column("convb", j)).then_inc(tap0, 1)
                else:
                    act.activation(silu_g[:, :], up_g[:, 2:S + 2], ACT.Silu).then_inc(silu_ready, 1)

            def tap_val(layer, j, chunk):
                if layer.n == 0:
                    act.wait_ge(chunk_out, chunk + 2)
                    act.activation(tap_v[:, :], up_v[:, 0:S], ACT.Identity, scale=column("conv0", FC + j),
                                   bias=column("convb", FC + j)).then_inc(tap0, 1)
                    act.wait_ge(taps, 4 * j + 2)
                    act.activation(silu_g[:, :], tap_g[:, :], ACT.Silu).then_inc(silu_ready, 1)

            def hidden_hi(layer, j):
                act.wait_ge(hid_ready, FC * layer.n + j + 1)
                act.activation(hid_hi[:, j, :], hid[:, :], ACT.Copy).then_inc(hid_hi_ready, 1)

            act.dma_start(vec[:, :], vectors).then_inc(vec_landed, 16)
            act.wait_ge(vec_landed, 16)
            for quarter in range(RING):
                act.wait_ge(x_landed[quarter], 16)
                for c in range(XQ * quarter, XQ * (quarter + 1)):
                    act.activation(xs_hi[:, c, :], xres[:, c, :], ACT.Copy, scale=column("norm0", c)).then_inc(xs_hi_ready, 1)
                if quarter != 1:
                    split_hi(Pos(0), max(quarter - 1, 0) - AHEAD)

            act.wait_ge(setup_done, 1)
            for s in range(2):
                split_hi(Pos(0), s)
                for c in range(KC // 2 * s, KC // 2 * (s + 1)):
                    if c >= 2:
                        act.wait_ge(sumsq, c - 1)
                    act.activation(sq_x[:, c % 2, :], xres[:, c, :], ACT.Square).then_inc(sq_ready, 1)

            def forget_gates():
                act.wait_ge(f_step, 3)
                act.activation(f_exp[0:FOX_HEADS, :], f_negabs[0:FOX_HEADS, :], ACT.Exp).then_inc(f_act, 1)
                act.wait_ge(f_act, 1)
                act.activation(f_ln[0:FOX_HEADS, :], f_exp[0:FOX_HEADS, :], ACT.Ln, bias=1.0).then_inc(f_act, 1)

            def softmax_heads(run, extra):
                for j in range(2):
                        for s in range(HEAD_UNITS):
                            if s == 0 and j:
                                head_rstd(run.count0)
                            split_hi(run.pos(0), HEAD_UNITS * j + s)
                            extra.get((j, s), lambda: None)()
                            head_step(run, run.count0 + j, run.mix0 + j, s, run.chunk0 + 3 * j, j)
                with act.Fori(1, run.n // 2) as i:
                    for j in range(2):
                        h = 2 * i + j
                        for s in range(HEAD_UNITS):
                            if s == 0:
                                head_rstd(run.count0 + h - 1)
                            split_hi(run.pos(i), HEAD_UNITS * j + s)
                            head_step(run, run.count0 + h, run.mix0 + h, s, run.chunk0 + 3 * h, 2)

            def project(layer, run):
                n = 2 * layer.n + 1
                head_rstd(run.count0 + run.n - 1)
                for s in range(8):
                    split_hi(Pos(layer.unit_out), s)
                    tail_step(run, s)
                    if s >= 5:
                        residual(n, s - 5, layer.chunk_out + s - 5)
                with act.Fori(1, KC // 4) as i:
                    pos = Pos(layer.unit_out, 8, i)
                    for s in range(8):
                        split_hi(pos, s)
                        if s == 0:
                            act.wait_ge(chunk_out, layer.chunk_out + 4 * i)
                            act.activation(xs_hi[:, 4 * i - 1, :], xres[:, 4 * i - 1, :], ACT.Copy,
                                           scale=column(f"norm{n}", 4 * i - 1)).then_inc(xs_hi_ready, 1)
                            act.activation(sq_x[:, 1, :], xres[:, 4 * i - 1, :], ACT.Square).then_inc(sq_ready, 1)
                        if s >= 5:
                            c = s - 5
                            act.wait_ge(chunk_out, layer.chunk_out + 4 * i + c + 1)
                            act.activation(xs_hi[:, 4 * i + c, :], xres[:, 4 * i + c, :], ACT.Copy,
                                           scale=column(f"norm{n}", 4 * i + c)).then_inc(xs_hi_ready, 1)
                            act.activation(sq_x[:, c % 2, :], xres[:, 4 * i + c, :], ACT.Square).then_inc(sq_ready, 1)

            def up(layer):
                def turn(pos, i, first):
                    for j in range(2):
                        pair = 2 * i + j
                        for s in range(4):
                            start = first and j == 0
                            split_hi(pos, 4 * j + s)
                            if start and s == 0:
                                residual(2 * layer.n + 1, KC - 1, layer.chunk_up - 1)
                            if start and s == 2:
                                norm_rstd(2 * layer.n + 1)
                            if s == 0 and not start:
                                tap_val(layer, pair - 1, layer.chunk_up + 2 * pair - 2)
                            if s == 1 and not start:
                                hidden_hi(layer, pair - 1)
                            if s == 3:
                                tap_gate(layer, pair, layer.chunk_up + 2 * pair)

                turn(Pos(layer.unit_up), 0, True)
                with act.Fori(1, FC // 2) as i:
                    turn(Pos(layer.unit_up, 8, i), i, False)

            def down_turn(layer, pos, i, first):
                done = {(FC * (c + 1) - 1) // BLOCKS + 1: c for c in range(8)}
                for k in range(U_DOWN // 2):
                    if pos.unit(k) + AHEAD < UNITS:
                        split_hi(pos, k)
                    if first and k == 0:
                        tap_val(layer, FC - 1, layer.chunk_down - 2)
                        hidden_hi(layer, FC - 1)
                    if not first and k == 0:
                        down_chunk(layer, i, -1)
                    if k in done:
                        down_chunk(layer, i, done[k])

            def down_chunk(layer, i, c):
                if layer.n == 0:
                    at = 8 * i + c
                    act.wait_ge(chunk_out, layer.chunk_down + at + 1)
                    act.activation(xs_hi[:, at, :], xres[:, at, :], ACT.Copy, scale=column("norm2", at)).then_inc(xs_hi_ready, 1)
                    act.activation(sq_x[:, c % 2, :], xres[:, at, :], ACT.Square).then_inc(sq_ready, 1)
                else:
                    at = 8 * i + c
                    act.wait_ge(chunk_out, layer.chunk_down + at + 1)
                    act.dma_start(out[:, at, :], xres[:, at, :]).then_inc(out_stored, 16)

            def down(layer):
                down_turn(layer, Pos(layer.unit_down), 0, True)
                down_turn(layer, Pos(layer.unit_down + U_DOWN // 2), 1, False)

            softmax_heads(FOX, {(0, 0): lambda: norm_rstd(0), (0, 2): forget_gates})
            project(L0, FOX)
            up(L0)
            down(L0)

            for s in range(2):
                split_hi(Pos(L1.unit_in), s)
                if s == 0:
                    residual(2, KC - 1, L1.chunk_in - 1)
            norm_rstd(2)

            def gate_logs():
                act.wait_ge(gate_step, 2)
                act.activation(g_t[:, :, :], g_t[:, :, :], ACT.Exp).then_inc(gate_act, 1)
                act.wait_ge(gate_act, 1)
                act.activation(g_t[:, :, :], g_t[:, :, :], ACT.Ln, bias=1.0).then_inc(gate_act, 1)

            def decays():
                act.wait_ge(gate_step, 5)
                act.activation(eb[:, :, :], g_l[:, :, :], ACT.Exp, scale=-1.0 / GLA_TAU).then_inc(gate_ready, 1)
                act.activation(enb[:, :, :], g_l[:, :, :], ACT.Exp, scale=1.0 / GLA_TAU).then_inc(gate_ready, 1)

            for s in range(GLA_UNITS):
                split_hi(Pos(L1.unit_heads), s)
                if s == 3:
                    gate_logs()
                if s == 5:
                    decays()
                gla_step(0, s, L1.chunk_heads, False)
            with act.Fori(1, GLA_HEADS) as g:
                for s in range(GLA_UNITS):
                    split_hi(Pos(L1.unit_heads, GLA_UNITS, g), s)
                    gla_step(g, s, L1.chunk_heads + 6 * g, True)
            softmax_heads(DIL, {(0, s): (lambda s=s: gla_step(GLA_HEADS, s, CHUNK_DIL, True, False)) for s in range(HEAD_UNITS)})
            project(L1, DIL)
            up(L1)
            down(L1)
            down_chunk(L1, 1, 7)

        @block.vector
        def _(dve):
            def split_lo(pos, k):
                k += AHEAD
                slot = pos.slot(k)
                dve.wait_ge(hi_ready, pos.unit(k) + 1)
                dve.tensor_tensor(wlo[slot][:, :], raw[slot][:, :], whi[slot][:, :], ALU.subtract).then_inc(lo_ready, 1)

            def add_residual(pos, k, c, chunk, bank_no):
                dve.wait_ge(unit_used, pos.unit(k))
                dve.tensor_tensor(xres[:, c, :], acc[bank_no][:, 0:S], xres[:, c, :], ALU.add).then_inc(chunk_out, 1)

            def norm_chunk(n, c, par, chunk_no):
                norm_lo(n, c, chunk_no)
                norm_sum(c, par, chunk_no)

            def norm_lo(n, c, chunk_no):
                dve.wait_ge(xs_hi_ready, chunk_no + 1)
                dve.scalar_tensor_tensor(out=xs_lo[:, c, :], in0=xres[:, c, :], scalar=column(f"norm{n}", c),
                                         in1=xs_hi[:, c, :], op0=ALU.mult, op1=ALU.subtract).then_inc(xs_ready, 1)

            def norm_sum(c, par, chunk_no):
                dve.wait_ge(sq_ready, chunk_no + 1)
                if isinstance(c, int) and c == 0:
                    dve.tensor_copy(sq_sum[:, :], sq_x[:, par, :]).then_inc(sumsq, 1)
                else:
                    dve.wait_ge(sumsq, chunk_no)
                    dve.tensor_tensor(sq_sum[:, :], sq_sum[:, :], sq_x[:, par, :], ALU.add).then_inc(sumsq, 1)

            def take(dst, bank_no, last_unit):
                dve.wait_ge(unit_used, last_unit + 1)
                rows = dst.shape[0]
                dve.tensor_tensor(dst, acc[bank_no][0:rows, 0:S], rstd[0:rows, :], ALU.mult).then_inc(chunk_out, 1)

            def norm_qk(run, n):
                dve.wait_ge(qk_rstd, n + 1)
                col = 0 if run.kind == "fox" else 2
                for a in range(2):
                    dve.scalar_tensor_tensor(out=qk_n[:, a, :], in0=qk[:, a, :], scalar=qk_gain[:, col + a:col + a + 1],
                                             in1=rstd_qk[:, a, :], op0=ALU.mult, op1=ALU.mult).then_inc(qk_ready, 1)

            def softmax_max(run, n, h):
                dve.wait_ge(scores_ready, n + 1)
                for t, (a, b) in enumerate(((0, P), (P, 3 * P))):
                    if run.kind == "fox":
                        table = decay_row[:, h, 0:b - a]
                    else:
                        table = toeplitz[:, h, S - (b - a):S]
                    dve.tensor_tensor(biased[:, a:b], b_score[:, a:b], table, ALU.add).then_inc(bias_added, 1)
                for t, (a, b) in enumerate(((0, P), (P, 3 * P))):
                    dve.wait_ge(bias_added, 2 * n + t + 1)
                    dve.tensor_reduce(stat[:, t, 0:1], biased[:, a:b], AX_X, ALU.max).then_inc(row_max, 1)
                for t in range(2):
                    dve.wait_ge(row_max, 2 * n + t + 1)
                    dve.tensor_scalar(stat[:, t, 1:2], stat[:, t, 0:1], -1.0, None, ALU.mult).then_inc(neg_max, 1)

            def softmax_norm(n):
                dve.wait_ge(exp_ready, 2 * n + 2)
                dve.reciprocal(stat[:, :, 3], stat[:, :, 2]).then_inc(row_inv, 1)
                dve.wait_ge(row_inv, n + 1)
                for t, (a, b) in enumerate(((0, P), (P, 3 * P))):
                    dve.tensor_scalar(probs[:, a:b], probs[:, a:b], stat[:, t, 3:4], None, ALU.mult).then_inc(probs_ready, 1)

            def copy_head(n):
                dve.wait_ge(head_ready, n + 1)
                dve.tensor_copy(head_o[:, :], b_mean[:, 0:S]).then_inc(head_copied, 1)

            def head_lo(n, at):
                dve.wait_ge(mix_hi_ready, n + 1)
                dve.tensor_tensor(mix_lo[:, at, :], head_o[:, :], mix_hi[:, at, :], ALU.subtract).then_inc(mix_ready, 1)

            def head_step(run, n, h, s, pos, k0, lag):
                at = run.mix0 + h
                if s == 0 and lag >= 1:
                    take(v_t[:, :], 3, pos.unit(k0 - 1))
                    norm_qk(run, n - 1)
                if s == 2:
                    if lag >= 2:
                        copy_head(n - 2)
                    if lag >= 1:
                        dve.wait_ge(qk_ready, 2 * n)
                    take(qk[:, 0, :], 1, pos.unit(k0 + 1))
                    if lag >= 1:
                        softmax_max(run, n - 1, h - 1)
                if s == 3 and lag >= 1:
                    softmax_norm(n - 1)
                if s == 3 and lag >= 2:
                    head_lo(n - 2, at - 2)
                if s == 4:
                    take(qk[:, 1, :], 2, pos.unit(k0 + 3))

            def tail_step(run, s, unit0):
                n, h = run.count0 + run.n, run.n
                at = run.mix0 + run.n
                if s == 0:
                    take(v_t[:, :], 3, unit0 - 1)
                    norm_qk(run, n - 1)
                if s == 1:
                    copy_head(n - 2)
                    softmax_max(run, n - 1, h - 1)
                if s == 2:
                    head_lo(n - 2, at - 2)
                    softmax_norm(n - 1)
                if s == 4:
                    copy_head(n - 1)
                    head_lo(n - 1, at - 1)

            def gla_step(g, s, pos, lag, own=True):
                chunk = lambda c: pos.unit(2 * c + 1)
                if s == 0 and lag:
                    take(g_r[:, 1, :], 3, pos.unit(-1))
                if s == 1 and lag:
                    dve.wait_ge(g_rstd, g)
                    for t in range(2):
                        dve.tensor_scalar(g_on[:, t, :], b_mean[:, t * GLA_DV:(t + 1) * GLA_DV], g_stat[:, t, 2:3], None,
                                          ALU.mult).then_inc(g_on_ready, 1)
                if s == 3 and lag:
                    dve.wait_ge(g_turned, g)
                    dve.wait_ge(g_silu_ready, g)
                    for c in range(2):
                        gate = dve.scalar_tensor_tensor(out=g_of[:, c, :], in0=b_val[:, c * S:(c + 1) * S], scalar=column("onorm", c),
                                                        in1=g_silu[:, c, :], op0=ALU.mult, op1=ALU.mult)
                    gate.then_inc(g_gated, 1)
                if s == 4 and lag:
                    dve.wait_ge(g_hi, g)
                    dve.tensor_tensor(mix_lo[:, bass.ds(2 * g - 2, 2), :], g_of[:, :, :], mix_hi[:, bass.ds(2 * g - 2, 2), :],
                                      ALU.subtract).then_inc(g_mixed, 1)
                if not own:
                    return
                if s == 2:
                    dve.wait_ge(unit_used, chunk(0) + 1)
                    dve.scalar_tensor_tensor(out=g_q[:, :], in0=acc[1][:, 0:S], scalar=float(P) ** -0.5, in1=rstd[:, :],
                                             op0=ALU.mult, op1=ALU.mult).then_inc(chunk_out, 1)
                if s == 4:
                    take(g_k[:, :], 2, chunk(1))
                if s == 6:
                    take(g_v[:, 0, :], 3, chunk(2))
                if s == 7:
                    if not lag:
                        dve.wait_ge(gate_ready, 2)
                    dve.wait_ge(chunk_out, L1.chunk_heads + 6 * g + 2)
                    dve.tensor_tensor(g_qt[:, :], g_q[:, :], eb[:, g, :], ALU.mult)
                    dve.tensor_tensor(g_kt[:, :], g_k[:, :], enb[:, g, :], ALU.mult).then_inc(gate_step, 1)
                    dve.wait_ge(gate_step, 6 + g)
                    ends = eb[:, g, :].rearrange("p (n c) -> p n c", c=GLA_CHUNK)[:, :, GLA_CHUNK - 1:GLA_CHUNK]
                    dve.tensor_tensor(g_kd[:, :].rearrange("p (n c) -> p n c", c=GLA_CHUNK),
                                      g_kt[:, :].rearrange("p (n c) -> p n c", c=GLA_CHUNK),
                                      ends.to_broadcast([P, S // GLA_CHUNK, GLA_CHUNK]), ALU.mult).then_inc(g_qk_ready, 1)
                if s == 8:
                    dve.wait_ge(g_intra, g + 1)
                    take(g_v[:, 1, :], 1, chunk(3))
                    for t in range(2):
                        keep = dve.copy_predicated(g_attn[:, t, :], g_mask[:, :], b_score[:, t * GLA_CHUNK:(t + 1) * GLA_CHUNK])
                    keep.then_inc(g_intra_ready, 1)
                if s == 10:
                    take(g_r[:, 0, :], 2, chunk(4))
                if s == 11:
                    dve.wait_ge(g_cs, g + 1)
                    dve.tensor_copy(g_state[:, 0, :], b_score[:, 0:GLA_DV]).then_inc(g_states, 1)
                    for n in (1, 2):
                        dve.wait_ge(g_states, 3 * g + n)
                        cs = b_turn[:, 0:GLA_DV] if n == 1 else b_score[:, GLA_DV:2 * GLA_DV]
                        dve.scalar_tensor_tensor(out=g_state[:, n, :], in0=g_state[:, n - 1, :],
                                                 scalar=eb[:, g, GLA_CHUNK * (n + 1) - 1:GLA_CHUNK * (n + 1)],
                                                 in1=cs, op0=ALU.mult, op1=ALU.add).then_inc(g_states, 1)

            def conv_taps(up_x, tap_x, c, count):
                dve.wait_ge(tap0, count + 1)
                dve.scalar_tensor_tensor(out=tap_x[:, :], in0=up_x[:, 1:S + 1], scalar=column("conv1", c), in1=tap_x[:, :],
                                         op0=ALU.mult, op1=ALU.add).then_inc(taps, 1)
                dve.wait_ge(taps, 2 * count + 1)
                dve.scalar_tensor_tensor(out=tap_x[:, :], in0=up_x[:, 2:S + 2], scalar=column("conv2", c), in1=tap_x[:, :],
                                         op0=ALU.mult, op1=ALU.add).then_inc(taps, 1)

            def take_val(layer, j, last_unit, bank_no):
                take(up_v[:, 2:S + 2], bank_no, last_unit)
                if layer.n == 0:
                    conv_taps(up_g, tap_g, j, 2 * j)

            def hidden(layer, j):
                if layer.n == 0:
                    conv_taps(up_v, tap_v, FC + j, 2 * j + 1)
                    dve.wait_ge(taps, 4 * j + 4)
                else:
                    dve.wait_ge(chunk_out, layer.chunk_up + 2 * j + 2)
                src = tap_v[:, :] if layer.n == 0 else up_v[:, 2:S + 2]
                dve.wait_ge(silu_ready, FC * layer.n + j + 1)
                dve.tensor_tensor(hid[:, :], silu_g[:, :], src, ALU.mult).then_inc(hid_ready, 1)

            def hid_low(layer, j):
                dve.wait_ge(hid_hi_ready, FC * layer.n + j + 1)
                dve.tensor_tensor(hid_lo[:, j, :], hid[:, :], hid_hi[:, j, :], ALU.subtract).then_inc(hid_split, 1)

            dve.memset(mean_d[:, :], 1.0 / D)
            dve.memset(mean_h[:, :], 1.0 / P)
            dve.memset(eps[:, :], EPS)
            dve.memset(up_g[:, :], 0.0)
            dve.memset(up_v[:, :], 0.0)
            dve.memset(f_one[:, :], 1.0)
            dve.memset(rel_sb[REL_BUCKETS:REL_BUCKETS + 1, :], 1.0)
            dve.wait_ge(vec_landed, 16)
            scale = float(P) ** -0.5
            for a, (name, by) in enumerate((("fox_q", scale), ("fox_k", 1.0), ("dil_q", scale), ("dil_k", 1.0))):
                last = dve.tensor_scalar(qk_gain[:, a:a + 1], column(name), by, None, ALU.mult)
            last.then_inc(setup_done, 1)
            for quarter in range(RING):
                for c in range(XQ * quarter, XQ * (quarter + 1)):
                    norm_lo(0, c, c)
                if quarter != 1:
                    split_lo(Pos(0), max(quarter - 1, 0) - AHEAD)

            for s in range(2):
                split_lo(Pos(0), s)
                for c in range(KC // 2 * s, KC // 2 * (s + 1)):
                    norm_sum(c, c % 2, c)

            def tables():
                dve.wait_ge(consts_landed, 16 * 4)
                dve.tensor_copy(ident_bf[:, :], ident[:, :])
                dve.tensor_copy(maskneg_bf[:, :], mask_sb[:, :]).then_inc(setup_done, 1)
                dve.wait_ge(bias_made, 1)
                dve.tensor_copy(dist_bias[:, :], b_score[0:DIL_HEADS, 0:TOEPLITZ]).then_inc(bias_out, 1)

            def forget_gates():
                r = slice(0, FOX_HEADS)
                dve.wait_ge(rstd_ready, 1)
                take(f_z[r, :], 0, 1)
                dve.wait_ge(chunk_out, 1)
                dve.tensor_scalar(f_z[r, :], f_z[r, :], column("fox_b")[r, :], None, ALU.add).then_inc(f_step, 1)
                dve.wait_ge(f_step, 1)
                dve.scalar_tensor_tensor(out=f_negabs[r, :], in0=f_z[r, :], scalar=-1.0, in1=f_z[r, :], op0=ALU.mult, op1=ALU.min).then_inc(f_step, 1)
                dve.tensor_scalar(f_neg[r, :], f_z[r, :], -1.0, 0.0, ALU.mult, ALU.max).then_inc(f_step, 1)

            def forget_sum():
                r = slice(0, FOX_HEADS)
                dve.wait_ge(f_act, 2)
                dve.wait_ge(f_step, 3)
                dve.tensor_tensor(f_neg[r, :], f_neg[r, :], f_ln[r, :], ALU.add).then_inc(f_step, 1)
                dve.wait_ge(f_step, 4)
                dve.tensor_tensor_scan(f_cum[r, :], f_one[r, :], f_neg[r, :], 0.0, ALU.mult, ALU.add).then_inc(decay_out, 1)

            def softmax_heads(run, extra):
                for j in range(2):
                    for s in range(HEAD_UNITS):
                        extra(j, s)
                        head_step(run, run.count0 + j, j, s, run.pos(0), HEAD_UNITS * j, j)
                        split_lo(run.pos(0), HEAD_UNITS * j + s)
                with dve.Fori(1, run.n // 2) as i:
                    for j in range(2):
                        h = 2 * i + j
                        for s in range(HEAD_UNITS):
                            head_step(run, run.count0 + h, h, s, run.pos(i), HEAD_UNITS * j, 2)
                            split_lo(run.pos(i), HEAD_UNITS * j + s)

            def project(layer, run):
                n = 2 * layer.n + 1
                base = KC * n
                pos = Pos(layer.unit_out)
                for s in range(8):
                    tail_step(run, s, layer.unit_out)
                    if s >= 5:
                        add_residual(pos, s, s - 5, layer.chunk_out + s - 5, s - 5)
                    split_lo(pos, s)
                    if s >= 5:
                        norm_chunk(n, s - 5, (s - 5) % 2, base + s - 5)
                with dve.Fori(1, KC // 4) as i:
                    pos = Pos(layer.unit_out, 8, i)
                    for s in range(8):
                        c = 3 - 4 if s == 0 else s - 5
                        if s == 0 or s >= 5:
                            add_residual(pos, s, 4 * i + c, 0, c % 4)
                        split_lo(pos, s)
                        if s == 0 or s >= 5:
                            norm_chunk(n, 4 * i + c, c % 2, base + 4 * i + c)

            def up(layer):
                n = 2 * layer.n + 1

                def turn(pos, i, first):
                    for j in range(2):
                        pair = 2 * i + j
                        for s in range(4):
                            k = 4 * j + s
                            start = first and j == 0
                            if start and s == 0:
                                add_residual(pos, 0, KC - 1, 0, 3)
                                norm_chunk(n, KC - 1, 1, KC * n + KC - 1)
                            if start and s == 3:
                                dve.wait_ge(rstd_ready, n + 1)
                            if s == 0 and not start:
                                take_val(layer, pair - 1, pos.unit(k - 1), (2 * j - 1) % 4)
                            if s == 1 and not start:
                                hidden(layer, pair - 1)
                            if s == 2 and not start:
                                hid_low(layer, pair - 1)
                            if s == 3:
                                take(up_g[:, 2:S + 2], 2 * j, pos.unit(k - 1))
                            split_lo(pos, k)

                turn(Pos(layer.unit_up), 0, True)
                with dve.Fori(1, FC // 2) as i:
                    turn(Pos(layer.unit_up, 8, i), i, False)

            def down(layer):
                done = {(FC * (c + 1) - 1) // BLOCKS + 1: c for c in range(8)}
                for i in range(2):
                    pos = Pos(layer.unit_down + i * U_DOWN // 2)
                    for k in range(U_DOWN // 2):
                        if i == 0 and k == 0:
                            take_val(layer, FC - 1, pos.unit(-1), 3)
                            hidden(layer, FC - 1)
                            hid_low(layer, FC - 1)
                        c = done.get(k, -1 if k == 0 and i else None)
                        if c is not None:
                            add_residual(pos, k, 8 * i + c, 0, c % 4)
                        if pos.unit(k) + AHEAD < UNITS:
                            split_lo(pos, k)
                        if c is not None and layer.n == 0:
                            norm_chunk(2, 8 * i + c, c % 2, 2 * KC + 8 * i + c)

            def fox_extra(j, s):
                if (j, s) == (0, 2):
                    forget_gates()
                if (j, s) == (0, 3):
                    tables()
                    forget_sum()
                if (j, s) == (1, 2):
                    dve.wait_ge(decay_landed, 16)

            softmax_heads(FOX, fox_extra)
            project(L0, FOX)
            dve.wait_ge(bias_stored, 16)
            up(L0)
            down(L0)

            for s in range(2):
                if s == 0:
                    add_residual(Pos(L1.unit_in), 0, KC - 1, 0, 3)
                    norm_chunk(2, KC - 1, 1, 3 * KC - 1)
                split_lo(Pos(L1.unit_in), s)

            def gate_ranks():
                dve.wait_ge(rstd_ready, 3)
                take(ga[:, :], 0, L1.unit_in + 1)
                dve.memset(g_attn[:, :, :], 0.0)

            def gate_decays():
                dve.wait_ge(gate_pre, 1)
                for g in range(GLA_HEADS):
                    z = dve.tensor_scalar(g_z[:, g, :], (b_score, b_turn)[g // 2][:, (g % 2) * S:(g % 2 + 1) * S],
                                          column("gate_b", g), None, ALU.add)
                z.then_inc(gate_step, 1)
                dve.wait_ge(gate_step, 1)
                dve.scalar_tensor_tensor(out=g_t[:, :, :], in0=g_z[:, :, :], scalar=-1.0, in1=g_z[:, :, :], op0=ALU.mult, op1=ALU.min).then_inc(gate_step, 1)
                dve.tensor_scalar(g_z[:, :, :], g_z[:, :, :], -1.0, 0.0, ALU.mult, ALU.max).then_inc(gate_step, 1)

            def gate_sums():
                dve.wait_ge(gate_act, 2)
                dve.wait_ge(gate_step, 3)
                dve.tensor_tensor(g_z[:, :, :], g_z[:, :, :], g_t[:, :, :], ALU.add).then_inc(gate_step, 1)
                dve.wait_ge(gate_step, 4)
                for g in range(GLA_HEADS):
                    scan = dve.tensor_tensor_scan(g_l[:, g, :], g_keep[:, :], g_z[:, g, :], 0.0, ALU.mult, ALU.add)
                scan.then_inc(gate_step, 1)

            for s in range(GLA_UNITS):
                if s == 0:
                    gate_ranks()
                if s == 3:
                    gate_decays()
                if s == 4:
                    gate_sums()
                gla_step(0, s, Pos(L1.unit_heads), False)
                split_lo(Pos(L1.unit_heads), s)
            with dve.Fori(1, GLA_HEADS) as g:
                for s in range(GLA_UNITS):
                    gla_step(g, s, Pos(L1.unit_heads, GLA_UNITS, g), True)
                    split_lo(Pos(L1.unit_heads, GLA_UNITS, g), s)

            def dil_extra(j, s):
                if j == 0:
                    gla_step(GLA_HEADS, s, Pos(DIL.unit0), True, False)
                if (j, s) == (1, 0):
                    dve.wait_ge(toeplitz_landed, 16 * DIL_HEADS)

            softmax_heads(DIL, dil_extra)
            project(L1, DIL)
            up(L1)
            down(L1)
            add_residual(Pos(UNITS), 0, KC - 1, 0, 3)


def shape_constants():
    span = 127 + P - np.arange(TOEPLITZ)
    pos = np.maximum(span, 0)
    exact = REL_BUCKETS // 2
    large = exact + (np.log(np.maximum(pos, 1) / exact) / np.log(REL_MAX_DIST / exact) * (REL_BUCKETS - exact)).astype(np.int64)
    bucket = np.where(pos < exact, pos, np.minimum(large, REL_BUCKETS - 1))
    times = sum(((span >= 0) & (span % d == 0) & (span <= w)).astype(int) for w, d in DIL_PATTERNS)
    onehot = np.zeros((REL_BUCKETS + 1, TOEPLITZ), np.float32)
    onehot[bucket, np.arange(TOEPLITZ)] = 1.0
    onehot[REL_BUCKETS] = np.where(times > 0, np.log(np.maximum(times, 1)), NEG_INF)
    scan_keep = np.ones((P, S), np.float32)
    scan_keep[:, ::GLA_CHUNK] = 0.0
    key, query = np.arange(P)[:, None] % GLA_CHUNK, np.arange(GLA_CHUNK)[None, :]
    above = np.arange(P)[None, :] > np.arange(P)[:, None]
    return {
        "identity": np.eye(P, dtype=np.float32),
        "dist_onehot": onehot,
        "scan_keep": scan_keep,
        "gla_mask": (key <= query).astype(np.int32),
        "fox_mask": np.where(above, NEG_INF, 0.0).astype(np.float32),
    }


def units_in(w, order):
    a = w.reshape(2, BLOCKS, P, -1, P).transpose(3, 0, 2, 1, 4)[order]
    return a.reshape(-1, P, BLOCKS, P)


def units_out(w):
    return w.reshape(2, BLOCKS, P, KC // 4, 4, P).transpose(3, 0, 4, 2, 1, 5).reshape(-1, P, BLOCKS, P)


def units_up(gate, val):
    a = np.stack([gate, val]).reshape(2, 2, BLOCKS, P, FC, P)
    return a.transpose(4, 1, 0, 3, 2, 5).reshape(-1, P, BLOCKS, P)


def units_down(w):
    a = w.reshape(FC, P, KC, P).transpose(2, 0, 1, 3).reshape(-1, BLOCKS, P, P)
    return a.transpose(0, 2, 1, 3)


def with_narrow(wide, narrow):
    fill = np.zeros((D, P - narrow.shape[1]), np.float32)
    return np.concatenate([wide, narrow, fill], axis=1)


def kernel(**inputs):
    import concourse.bacc as bacc
    from concourse.bass_utils import run_bass_kernel_spmd

    a = {k: np.asarray(v) for k, v in inputs.items()}
    hd = FOX_HEADS * P
    fox_order = [3 * FOX_HEADS] + [FOX_HEADS * part + h for h in range(FOX_HEADS) for part in range(3)]
    w1 = with_narrow(a["fox_w_in"][0][:, :3 * hd], a["fox_w_in"][0][:, 3 * hd:])
    w2 = a["w_in_2"][0]
    cut = 2 * GLA_HEADS * P + 2 * GLA_HEADS * GLA_DV
    w2 = with_narrow(np.concatenate([w2[:, :cut], w2[:, cut + 16:]], axis=1), w2[:, cut:cut + 16])
    second = [IN_CHUNKS - 1]
    for g in range(GLA_HEADS):
        second += [g, 4 + g, 8 + 2 * g, 9 + 2 * g, 16 + 2 * g, 17 + 2 * g]
    second += [24 + DIL_HEADS * part + h for h in range(DIL_HEADS) for part in range(3)]
    up = a["ffn_w_up"][0]
    wstream = np.concatenate([
        units_in(w1, fox_order), units_out(a["fox_w_out"][0]), units_up(up[:, :FF], up[:, FF:]), units_down(a["ffn_w_down"][0]),
        units_in(w2, second), units_out(a["w_out_2"][0]), units_up(a["w_gate_2"][0], a["w_up_2"][0]), units_down(a["w_down_2"][0]),
    ]).reshape(UNITS, P, UW)

    def cols(v):
        return v.reshape(-1, P).T

    fox_b = np.zeros((P, 1), np.float32)
    fox_b[:FOX_HEADS, 0] = a["fox_b_f"][0]
    vectors = np.concatenate([
        cols(a["mix_norm"][0]), cols(a["ffn_norm"][0]), cols(a["norm1_g_2"][0]), cols(a["norm2_g_2"][0]),
        cols(a["ffn_conv_w"][0, 0]), cols(a["ffn_conv_w"][0, 1]), cols(a["ffn_conv_w"][0, 2]), cols(a["ffn_conv_b"][0]),
        cols(a["fox_q_gain"][0]), cols(a["fox_k_gain"][0]), cols(a["q_norm_g_2"][0]), cols(a["k_norm_g_2"][0]),
        cols(a["gla_onorm_g_2"][0]), cols(a["gla_gate_b_2"][0]), fox_b], axis=1)
    arrays = {
        "wstream": wstream,
        "xt": np.ascontiguousarray(a["x"][0].reshape(S, KC, P).transpose(2, 1, 0)),
        "vectors": np.ascontiguousarray(vectors),
        "rel_bias": np.ascontiguousarray(a["rel_bias_2"]),
        "gate_w2": np.ascontiguousarray(a["gla_gate_w2_2"][0]),
        **shape_constants(),
    }
    nc = bacc.Bacc("TRN2", target_bir_lowering=False, num_devices=1)
    aps = {}
    for name, v in arrays.items():
        aps[name] = nc.dram_tensor(name, v.shape, mybir.dt.from_np(v.dtype), kind="ExternalInput").ap()
    aps["out"] = nc.dram_tensor("out", (P, KC, S), F32, kind="ExternalOutput").ap()
    build(nc, **aps)
    got = run_bass_kernel_spmd(nc, [arrays], core_ids=[0]).results[0]["out"]
    return got.transpose(2, 1, 0).reshape(1, S, D)
```
